# Optimizing a Trainium2 kernel written in Bass

```python
import jax, jax.numpy as jnp
from jax import lax
import numpy as np

D_MODEL = 1024
BATCH = 1
SEQ = 256
DEPTH = 2

HEAD_DIM = 64
NA_HEADS = 8
GQA_Q_HEADS = 8
GQA_KV_HEADS = 2
GRID_W = 64
NA_WIN_ROWS = 8
NA_WIN_COLS = 16
SWA_WINDOW = 128
SWA_BLOCK = 128
ROPE_THETA = 10000.0
PEER_HEADS = 8
PEER_N_KEYS = 128
PEER_N_EXPERTS = PEER_N_KEYS * PEER_N_KEYS
PEER_TOPK = 16
PEER_KEY_DIM = 256
PEER_CHUNK = 128
N_BRANCH = 2
EPS = 1e-6

NA_WIDTH = NA_HEADS * HEAD_DIM
GQA_Q_WIDTH = GQA_Q_HEADS * HEAD_DIM
GQA_KV_WIDTH = GQA_KV_HEADS * HEAD_DIM
IN_SPLITS = (NA_WIDTH, 2 * NA_WIDTH, 3 * NA_WIDTH,
             3 * NA_WIDTH + GQA_Q_WIDTH,
             3 * NA_WIDTH + GQA_Q_WIDTH + GQA_KV_WIDTH,
             3 * NA_WIDTH + GQA_Q_WIDTH + 2 * GQA_KV_WIDTH)
IN_COLS = IN_SPLITS[-1] + N_BRANCH * D_MODEL


def rms_norm(x, g):
    xf = x.astype(jnp.float32)
    y = xf * lax.rsqrt(jnp.mean(xf * xf, axis=-1, keepdims=True) + EPS)
    return (y * g.astype(jnp.float32)).astype(x.dtype)

def rotary(x, pos):
    half = x.shape[-1] // 2
    inv = ROPE_THETA ** (-jnp.arange(half, dtype=jnp.float32) / half)
    ang = pos.astype(jnp.float32)[:, None] * inv[None, :]
    cos = jnp.cos(ang)[None, :, None, :]
    sin = jnp.sin(ang)[None, :, None, :]
    xf = x.astype(jnp.float32)
    x1, x2 = xf[..., :half], xf[..., half:]
    out = jnp.concatenate([x1 * cos - x2 * sin, x1 * sin + x2 * cos], axis=-1)
    return out.astype(x.dtype)

def neighbourhood_attention(q, k, v, rpb):
    B, S, H, dh = q.shape
    rows = S // GRID_W
    kr = min(NA_WIN_ROWS, rows)
    r = jnp.arange(rows)
    rs = jnp.clip(r - kr // 2, 0, rows - kr)
    key_rows = rs[:, None] + jnp.arange(kr)[None, :]
    c = jnp.arange(GRID_W)
    cs = jnp.clip(c - NA_WIN_COLS // 2, 0, GRID_W - NA_WIN_COLS)
    qg = q.reshape(B, rows, GRID_W, H, dh)
    kg = k.reshape(B, rows, GRID_W, H, dh)[:, key_rows]
    vg = v.reshape(B, rows, GRID_W, H, dh)[:, key_rows]
    s = jnp.einsum('brqhd,brakhd->brhqak', qg, kg).astype(jnp.float32) * (dh ** -0.5)
    dr_idx = key_rows - r[:, None] + (NA_WIN_ROWS - 1)
    dc = c[None, :] - c[:, None]
    dc_idx = jnp.clip(dc + NA_WIN_COLS - 1, 0, 2 * NA_WIN_COLS - 2)
    in_win = (c[None, :] >= cs[:, None]) & (c[None, :] < cs[:, None] + NA_WIN_COLS)
    bias = rpb.astype(jnp.float32)[:, dr_idx[:, None, :, None], dc_idx[None, :, None, :]]
    bias = jnp.where(in_win[:, None, :], jnp.transpose(bias, (1, 0, 2, 3, 4)), -jnp.inf)
    p = jax.nn.softmax(s + bias[None], axis=(-2, -1))
    o = jnp.einsum('brhqak,brakhd->brqhd', p.astype(v.dtype), vg)
    return o.reshape(B, S, H * dh)

def sliding_window_gqa(q, k, v, sink):
    B, S, Hq, dh = q.shape
    Hkv = k.shape[2]
    G = Hq // Hkv
    nb = S // SWA_BLOCK
    pad = ((0, 0), (SWA_BLOCK, SWA_BLOCK), (0, 0), (0, 0))
    kp = jnp.pad(k, pad).reshape(B, nb + 2, SWA_BLOCK, Hkv, dh)
    vp = jnp.pad(v, pad).reshape(B, nb + 2, SWA_BLOCK, Hkv, dh)
    kw = jnp.concatenate([kp[:, :-2], kp[:, 1:-1], kp[:, 2:]], axis=2)
    vw = jnp.concatenate([vp[:, :-2], vp[:, 1:-1], vp[:, 2:]], axis=2)
    qb = q.reshape(B, nb, SWA_BLOCK, Hkv, G, dh)
    s = jnp.einsum('bnqkgd,bnckd->bnkgqc', qb, kw).astype(jnp.float32) * (dh ** -0.5)
    blk = jnp.arange(nb)[:, None]
    qpos = blk * SWA_BLOCK + jnp.arange(SWA_BLOCK)[None, :]
    kpos = (blk - 1) * SWA_BLOCK + jnp.arange(3 * SWA_BLOCK)[None, :]
    valid = ((kpos >= 0) & (kpos < S))[:, None, :] & \
        (jnp.abs(qpos[:, :, None] - kpos[:, None, :]) <= SWA_WINDOW)
    s = jnp.where(valid[None, :, None, None], s, -jnp.inf)
    sink_l = jnp.broadcast_to(sink.astype(jnp.float32).reshape(Hkv, G)[None, None, :, :, None, None],
                              s.shape[:-1] + (1,))
    p = jax.nn.softmax(jnp.concatenate([s, sink_l], axis=-1), axis=-1)[..., :-1]
    o = jnp.einsum('bnkgqc,bnckd->bnqkgd', p.astype(v.dtype), vw)
    return o.reshape(B, S, Hq * dh)

def token_mixer(h, w_in, gate_bias, qk_norm, na_rpb, swa_sink, w_branch_na, w_branch_swa, w_out, pos):
    B, S, _ = h.shape
    proj = h @ w_in
    qa, ka, va, qb, kb, vb, gl = jnp.split(proj, IN_SPLITS, axis=-1)
    heads = lambda t, n: t.reshape(B, S, n, HEAD_DIM)
    qa = rms_norm(heads(qa, NA_HEADS), qk_norm[0])
    ka = rms_norm(heads(ka, NA_HEADS), qk_norm[1])
    va = heads(va, NA_HEADS)
    qb = rotary(rms_norm(heads(qb, GQA_Q_HEADS), qk_norm[2]), pos)
    kb = rotary(rms_norm(heads(kb, GQA_KV_HEADS), qk_norm[3]), pos)
    vb = heads(vb, GQA_KV_HEADS)
    oa = neighbourhood_attention(qa, ka, va, na_rpb)
    ob = sliding_window_gqa(qb, kb, vb, swa_sink)
    gates = jax.nn.sigmoid((gl.reshape(B, S, N_BRANCH, D_MODEL) + gate_bias).astype(jnp.float32)).astype(h.dtype)
    merged = gates[:, :, 0] * (oa @ w_branch_na) + gates[:, :, 1] * (ob @ w_branch_swa)
    return merged @ w_out

def peer_ffn(x, w_query, sub_keys, expert_down, expert_up):
    B, S, D = x.shape
    T = B * S
    half = PEER_KEY_DIM // 2

    def chunk(xc):
        q = (xc @ w_query).reshape(PEER_CHUNK, PEER_HEADS, 2, half)
        s = jnp.einsum('thpk,pnk->thpn', q, sub_keys).astype(jnp.float32)
        sv, si = lax.top_k(s, PEER_TOPK)
        cand = (sv[:, :, 0, :, None] + sv[:, :, 1, None, :]).reshape(PEER_CHUNK, PEER_HEADS, PEER_TOPK * PEER_TOPK)
        cidx = (si[:, :, 0, :, None] * PEER_N_KEYS + si[:, :, 1, None, :]).reshape(PEER_CHUNK, PEER_HEADS, PEER_TOPK * PEER_TOPK)
        top_s, sel = lax.top_k(cand, PEER_TOPK)
        eidx = jnp.take_along_axis(cidx, sel, axis=-1)
        g = jax.nn.softmax(top_s, axis=-1)
        u = expert_down[eidx]
        vv = expert_up[eidx]
        act = jax.nn.gelu(jnp.einsum('td,thkd->thk', xc, u).astype(jnp.float32), approximate=False)
        return jnp.einsum('thk,thkd->td', (g * act).astype(x.dtype), vv)

    out = lax.map(chunk, x.reshape(T // PEER_CHUNK, PEER_CHUNK, D))
    return out.reshape(B, S, D)

def first_inputs(seed: int = 0) -> dict:
    key = jax.random.key(seed)
    ks = jax.random.split(key, 16)
    f32 = jnp.float32

    def nrm(k, shape, scale):
        return jax.random.normal(k, shape, f32) * scale

    return {
        "x": nrm(ks[0], (BATCH, SEQ, D_MODEL), 1.0),
        "norm_mix": 1.0 + nrm(ks[1], (DEPTH, D_MODEL), 0.02),
        "w_in": nrm(ks[2], (DEPTH, D_MODEL, IN_COLS), D_MODEL ** -0.5),
        "gate_bias": nrm(ks[3], (DEPTH, N_BRANCH, D_MODEL), 0.02),
        "qk_norm": 1.0 + nrm(ks[4], (DEPTH, 4, HEAD_DIM), 0.02),
        "na_rpb": nrm(ks[5], (DEPTH, NA_HEADS, 2 * NA_WIN_ROWS - 1, 2 * NA_WIN_COLS - 1), 0.1),
        "swa_sink": nrm(ks[6], (DEPTH, GQA_Q_HEADS), 0.5),
        "w_branch_na": nrm(ks[7], (DEPTH, NA_WIDTH, D_MODEL), NA_WIDTH ** -0.5),
        "w_branch_swa": nrm(ks[8], (DEPTH, GQA_Q_WIDTH, D_MODEL), GQA_Q_WIDTH ** -0.5),
        "w_out": nrm(ks[9], (DEPTH, D_MODEL, D_MODEL), D_MODEL ** -0.5),
        "norm_ffn": 1.0 + nrm(ks[10], (DEPTH, D_MODEL), 0.02),
        "peer_query": nrm(ks[11], (DEPTH, D_MODEL, PEER_HEADS * PEER_KEY_DIM), D_MODEL ** -0.5),
        "peer_sub_keys": nrm(ks[12], (DEPTH, 2, PEER_N_KEYS, PEER_KEY_DIM // 2), (PEER_KEY_DIM // 2) ** -0.5),
        "peer_down": nrm(ks[13], (DEPTH, PEER_N_EXPERTS, D_MODEL), D_MODEL ** -0.5),
        "peer_up": nrm(ks[14], (DEPTH, PEER_N_EXPERTS, D_MODEL), (PEER_HEADS * PEER_TOPK) ** -0.5),
    }

def first_block(x, norm_mix, w_in, gate_bias, qk_norm, na_rpb, swa_sink, w_branch_na, w_branch_swa,
              w_out, norm_ffn, peer_query, peer_sub_keys, peer_down, peer_up):
    S = x.shape[1]
    pos = jnp.arange(S, dtype=jnp.int32)
    for l in range(DEPTH):
        x = x + token_mixer(rms_norm(x, norm_mix[l]), w_in[l], gate_bias[l], qk_norm[l], na_rpb[l],
                            swa_sink[l], w_branch_na[l], w_branch_swa[l], w_out[l], pos)
        x = x + peer_ffn(rms_norm(x, norm_ffn[l]), peer_query[l], peer_sub_keys[l], peer_down[l], peer_up[l])
    return x


CTX_LEN = 256
D_MIX = D_MODEL
W_ATTN = D_MIX // 4
W_FOURIER = D_MIX // 4
W_CONV = D_MIX // 4
W_POOL = D_MIX // 4
N_Q_HEADS = W_ATTN // HEAD_DIM
N_KV_HEADS = 2
Q_PER_KV = N_Q_HEADS // N_KV_HEADS
N_FOURIER_HEADS = 4
FOURIER_HEAD_DIM = W_FOURIER // N_FOURIER_HEADS
CONV_WIDTH = 31
POOL_WINDOWS = (2, 4, 8, 16)
POOL_GROUP = W_POOL // len(POOL_WINDOWS)
D_FF = -(-(8 * D_MODEL) // (3 * 256)) * 256
Q_BLOCK = 128
ATTN_SCALE = HEAD_DIM ** -0.5

OFF_Q = 0
OFF_K = OFF_Q + N_Q_HEADS * HEAD_DIM
OFF_V = OFF_K + N_KV_HEADS * HEAD_DIM
OFF_F = OFF_V + N_KV_HEADS * HEAD_DIM
OFF_C = OFF_F + W_FOURIER
OFF_P = OFF_C + 2 * W_CONV
D_IN = OFF_P + W_POOL


def rms_norm_2(x, g):
    xf = x.astype(jnp.float32)
    y = xf * lax.rsqrt(jnp.mean(xf * xf, axis=-1, keepdims=True) + EPS)
    return (y * g.astype(jnp.float32)).astype(x.dtype)

def layer_norm(x, g, b):
    xf = x.astype(jnp.float32)
    xc = xf - jnp.mean(xf, axis=-1, keepdims=True)
    y = xc * lax.rsqrt(jnp.mean(xc * xc, axis=-1, keepdims=True) + EPS)
    return (y * g.astype(jnp.float32) + b.astype(jnp.float32)).astype(x.dtype)

def axial_rope_tables(n, dtype):
    rows = n // GRID_W
    row = jnp.repeat(jnp.arange(rows, dtype=jnp.float32), GRID_W)
    col = jnp.tile(jnp.arange(GRID_W, dtype=jnp.float32), rows)
    n_freq = HEAD_DIM // 4
    inv_freq = ROPE_THETA ** (-jnp.arange(n_freq, dtype=jnp.float32) / n_freq)
    ang = jnp.concatenate([row[:, None] * inv_freq, col[:, None] * inv_freq], axis=-1)
    return jnp.cos(ang).astype(dtype), jnp.sin(ang).astype(dtype)

def apply_rope(x, cos, sin):
    xp = x.reshape(x.shape[:-1] + (HEAD_DIM // 2, 2))
    x0, x1 = xp[..., 0], xp[..., 1]
    cs = cos[None, :, None, :]
    sn = sin[None, :, None, :]
    return jnp.stack([x0 * cs - x1 * sn, x0 * sn + x1 * cs], axis=-1).reshape(x.shape)

def q_heads(pq, q_g):
    b, n, _ = pq.shape
    return rms_norm_2(pq.reshape(b, n, N_Q_HEADS, HEAD_DIM), q_g)

def kv_heads(pkv, k_g):
    b, n, _ = pkv.shape
    kv = pkv.reshape(b, n, 2, N_KV_HEADS, HEAD_DIM)
    return rms_norm_2(kv[:, :, 0], k_g), kv[:, :, 1]

def attend(q, k, v):
    b, nq = q.shape[:2]
    qg = q.reshape(b, nq, N_KV_HEADS, Q_PER_KV, HEAD_DIM)
    s = jnp.einsum('bqhgd,bkhd->bhgqk', qg, k).astype(jnp.float32) * ATTN_SCALE
    p = jax.nn.softmax(s, axis=-1).astype(v.dtype)
    o = jnp.einsum('bhgqk,bkhd->bqhgd', p, v)
    return o.reshape(b, nq, N_Q_HEADS * HEAD_DIM)

def attend_query_blocks(q, k, v):
    b, n = q.shape[:2]
    nb = n // Q_BLOCK
    qb = jnp.swapaxes(q.reshape(b, nb, Q_BLOCK, N_Q_HEADS, HEAD_DIM), 0, 1)
    ob = lax.map(lambda qi: attend(qi, k, v), qb)
    return jnp.swapaxes(ob, 0, 1).reshape(b, n, N_Q_HEADS * HEAD_DIM)

def fourier_mixer(u, w_f):
    b, n, _ = u.shape
    uf = u.astype(jnp.float32).reshape(b, n, N_FOURIER_HEADS, FOURIER_HEAD_DIM)
    y = jnp.fft.fft2(uf, axes=(1, 3), norm='ortho').real
    return y.reshape(b, n, W_FOURIER).astype(u.dtype) @ w_f

def conv_module(a, dw_w, dw_b, ln_g, ln_b, w_pw):
    glu = a[..., :W_CONV] * jax.nn.sigmoid(a[..., W_CONV:])
    y = lax.conv_general_dilated(
        glu, dw_w[:, None, :], window_strides=(1,),
        padding=[(CONV_WIDTH // 2, CONV_WIDTH // 2)],
        dimension_numbers=('NWC', 'WIO', 'NWC'),
        feature_group_count=W_CONV) + dw_b
    y = jax.nn.silu(layer_norm(y, ln_g, ln_b))
    return y @ w_pw

def pool_mixer(u, w_pool, scale):
    b, n, _ = u.shape
    uf = u.astype(jnp.float32)
    csum = jnp.concatenate([jnp.zeros((b, 1, W_POOL), jnp.float32), jnp.cumsum(uf, axis=1)], axis=1)
    t = jnp.arange(n)
    groups = []
    for gi, win in enumerate(POOL_WINDOWS):
        sl = slice(gi * POOL_GROUP, (gi + 1) * POOL_GROUP)
        lo = jnp.clip(t - win // 2, 0, n)
        hi = jnp.clip(t - win // 2 + win, 0, n)
        cs = csum[..., sl]
        cnt = (hi - lo).astype(jnp.float32)[None, :, None]
        mean = (jnp.take(cs, hi, axis=1) - jnp.take(cs, lo, axis=1)) / cnt
        groups.append(mean - uf[..., sl])
    y = jnp.stack(groups, axis=2).astype(u.dtype)
    y = jnp.einsum('blgc,gcd->blgd', y, w_pool).reshape(b, n, W_POOL)
    return y * scale

def swiglu(x, w_in, w_out):
    a, g = jnp.split(x @ w_in, 2, axis=-1)
    return (jax.nn.silu(a) * g) @ w_out

def mixers_and_ffn(x, p, attn, gate1, shift2, scale2, gate2, g2, w_f, dw_w, dw_b,
                   ln_g, ln_b, w_pw, w_pl, pl_scale, w_o, w_fi, w_fo):
    four = fourier_mixer(p[..., OFF_F:OFF_C], w_f)
    conv = conv_module(p[..., OFF_C:OFF_P], dw_w, dw_b, ln_g, ln_b, w_pw)
    pool = pool_mixer(p[..., OFF_P:], w_pl, pl_scale)
    mix = jnp.concatenate([attn, four, conv, pool], axis=-1) @ w_o
    x = x + gate1 * mix
    xn = rms_norm_2(x, g2) * (1 + scale2) + shift2
    return x + gate2 * swiglu(xn, w_fi, w_fo)

def second_inputs(seed: int = 0) -> dict:
    key = jax.random.key(seed)
    ks = jax.random.split(key, 24)
    f32 = jnp.float32
    L = DEPTH
    D = D_MODEL

    def nrm(k, shape, scale):
        return jax.random.normal(k, shape, f32) * scale

    return {
        'x': nrm(ks[0], (BATCH, SEQ, D), 1.0),
        'c': nrm(ks[1], (BATCH, D), 1.0),
        'ctx': nrm(ks[2], (BATCH, CTX_LEN, D), 1.0),
        'c_ctx': nrm(ks[3], (D,), 1.0),
        'w_mod': nrm(ks[4], (L, D, 6 * D), D ** -0.5),
        'b_mod': nrm(ks[5], (L, 6 * D), 0.02),
        'g_norm1': 1.0 + nrm(ks[6], (L, D), 0.02),
        'g_norm2': 1.0 + nrm(ks[7], (L, D), 0.02),
        'w_in': nrm(ks[8], (L, D, D_IN), D ** -0.5),
        'q_norm_g': 1.0 + nrm(ks[9], (L, HEAD_DIM), 0.02),
        'k_norm_g': 1.0 + nrm(ks[10], (L, HEAD_DIM), 0.02),
        'w_fourier': nrm(ks[11], (L, W_FOURIER, W_FOURIER), W_FOURIER ** -0.5),
        'conv_dw_w': nrm(ks[12], (L, CONV_WIDTH, W_CONV), CONV_WIDTH ** -0.5),
        'conv_dw_b': nrm(ks[13], (L, W_CONV), 0.02),
        'conv_ln_g': 1.0 + nrm(ks[14], (L, W_CONV), 0.02),
        'conv_ln_b': nrm(ks[15], (L, W_CONV), 0.02),
        'w_conv_pw': nrm(ks[16], (L, W_CONV, W_CONV), W_CONV ** -0.5),
        'w_pool': nrm(ks[17], (L, len(POOL_WINDOWS), POOL_GROUP, POOL_GROUP), POOL_GROUP ** -0.5),
        'pool_scale': 1.0 + nrm(ks[18], (L, W_POOL), 0.02),
        'w_out': nrm(ks[19], (L, D_MIX, D), D_MIX ** -0.5),
        'w_ffn_in': nrm(ks[20], (L, D, 2 * D_FF), D ** -0.5),
        'w_ffn_out': nrm(ks[21], (L, D_FF, D), D_FF ** -0.5),
    }

def second_block(x, c, ctx, c_ctx, w_mod, b_mod, g_norm1, g_norm2, w_in, q_norm_g, k_norm_g,
              w_fourier, conv_dw_w, conv_dw_b, conv_ln_g, conv_ln_b, w_conv_pw, w_pool,
              pool_scale, w_out, w_ffn_in, w_ffn_out):
    n = x.shape[1]
    cos, sin = axial_rope_tables(n, x.dtype)
    h = ctx
    sc = jax.nn.silu(c)
    scc = jax.nn.silu(c_ctx)
    for l in range(DEPTH):
        last = l == DEPTH - 1
        mod = jnp.split(sc @ w_mod[l] + b_mod[l], 6, axis=-1)
        shift1, scale1, gate1, shift2, scale2, gate2 = [m[:, None, :] for m in mod]
        n_ctx_mod = 2 if last else 6
        mod_c = jnp.split(scc @ w_mod[l][:, :n_ctx_mod * D_MODEL] + b_mod[l][:n_ctx_mod * D_MODEL], n_ctx_mod)

        hn = rms_norm_2(h, g_norm1[l]) * (1 + mod_c[1]) + mod_c[0]
        if last:
            kc, vc = kv_heads(hn @ w_in[l][:, OFF_K:OFF_F], k_norm_g[l])
        else:
            pc = hn @ w_in[l]
            qc = q_heads(pc[..., OFF_Q:OFF_K], q_norm_g[l])
            kc, vc = kv_heads(pc[..., OFF_K:OFF_F], k_norm_g[l])

        xn = rms_norm_2(x, g_norm1[l]) * (1 + scale1) + shift1
        p = xn @ w_in[l]
        q = apply_rope(q_heads(p[..., OFF_Q:OFF_K], q_norm_g[l]), cos, sin)
        k, v = kv_heads(p[..., OFF_K:OFF_F], k_norm_g[l])
        k = apply_rope(k, cos, sin)
        attn = attend_query_blocks(q, jnp.concatenate([kc, k], axis=1), jnp.concatenate([vc, v], axis=1))
        x_new = mixers_and_ffn(x, p, attn, gate1, shift2, scale2, gate2, g_norm2[l],
                               w_fourier[l], conv_dw_w[l], conv_dw_b[l], conv_ln_g[l], conv_ln_b[l],
                               w_conv_pw[l], w_pool[l], pool_scale[l], w_out[l], w_ffn_in[l], w_ffn_out[l])
        if not last:
            attn_c = attend(qc, kc, vc)
            h = mixers_and_ffn(h, pc, attn_c, mod_c[2], mod_c[3], mod_c[4], mod_c[5], g_norm2[l],
                               w_fourier[l], conv_dw_w[l], conv_dw_b[l], conv_ln_g[l], conv_ln_b[l],
                               w_conv_pw[l], w_pool[l], pool_scale[l], w_out[l], w_ffn_in[l], w_ffn_out[l])
        x = x_new
    return x


def setup_inputs(seed=0):
    out = dict(first_inputs(seed))
    for name, value in second_inputs(seed + 1).items():
        if name != "x":
            out[name + "_2"] = value
    return out


def reference(
    x, norm_mix, w_in, gate_bias, qk_norm, na_rpb, swa_sink, w_branch_na, w_branch_swa, w_out,
    norm_ffn, peer_query, peer_sub_keys, peer_down, peer_up, c_2, ctx_2, c_ctx_2, w_mod_2,
    b_mod_2, g_norm1_2, g_norm2_2, w_in_2, q_norm_g_2, k_norm_g_2, w_fourier_2, conv_dw_w_2,
    conv_dw_b_2, conv_ln_g_2, conv_ln_b_2, w_conv_pw_2, w_pool_2, pool_scale_2, w_out_2,
    w_ffn_in_2, w_ffn_out_2,
):
    x = first_block(
        x, norm_mix, w_in, gate_bias, qk_norm, na_rpb, swa_sink, w_branch_na, w_branch_swa,
        w_out, norm_ffn, peer_query, peer_sub_keys, peer_down, peer_up,
    )
    return second_block(
        x, c_2, ctx_2, c_ctx_2, w_mod_2, b_mod_2, g_norm1_2, g_norm2_2, w_in_2, q_norm_g_2,
        k_norm_g_2, w_fourier_2, conv_dw_w_2, conv_dw_b_2, conv_ln_g_2, conv_ln_b_2,
        w_conv_pw_2, w_pool_2, pool_scale_2, w_out_2, w_ffn_in_2, w_ffn_out_2,
    )


_drawn_inputs = setup_inputs


def setup_inputs(seed=0):
    import zlib

    import numpy as np

    out = dict(_drawn_inputs(seed))
    spreads = {}
    factors = {'norm_mix': 6.101,
     'gate_bias': 8.0,
     'qk_norm': 7.759,
     'na_rpb': 3.153,
     'swa_sink': 8.0,
     'norm_ffn': 5.435,
     'g_norm1_2': 5.109,
     'g_norm2_2': 10.591,
     'q_norm_g_2': 8.0,
     'k_norm_g_2': 8.0,
     'conv_dw_b_2': 55.588,
     'conv_ln_g_2': 64.0,
     'conv_ln_b_2': 64.0,
     'pool_scale_2': 7.326}
    for name, (base, spread) in spreads.items():
        noise = np.random.default_rng([zlib.crc32(name.encode()), seed]).standard_normal(out[name].shape)
        drawn = base * np.exp(spread * noise) if base else spread * noise
        out[name] = __import__('jax').numpy.asarray(drawn.astype(out[name].dtype))
    for name, factor in factors.items():
        out[name] = (out[name] * factor).astype(out[name].dtype)
    return out
```

```python
import math
from contextlib import ExitStack

import numpy as np
import concourse.bass as bass
from concourse import mybir

FP32 = mybir.dt.float32
U32 = mybir.dt.uint32
ALU = mybir.AluOpType
ACT = mybir.ActivationFunctionType
AX = mybir.AxisListType

P = 128
D = 1024
KD = D // P
T = 256
TT = T // P
DEPTH = 2
EPS = 1e-6
HD = 64
NA_HEADS = 8
GQA_HEADS = 8
GRID_W = 64
GRID_H = T // GRID_W
WIN_ROWS, WIN_COLS = 8, 16
SWA_WINDOW = 128
THETA = 10000.0
KEYS = 128
TOPK = 16
PEER_HEADS = 8
HALVES = 2 * PEER_HEADS
CONV = 31
CONV_PAD = CONV // 2
POOL_WINDOWS = (2, 4, 8, 16)
D_FF = 2816
KF = D_FF // P
N_MOD = 6 * KD
SCALE = HD ** -0.5
MASKED = -1e30

BT = 16
RING = 4
N_QK1, N_V1, N_GATE = 13, 5, 2 * KD
N_FM2, N_TM2 = 9, 3
GQA_ORDER = [h for pair in zip(range(4), range(4, 8)) for h in pair]
ATT2_ORDER = [0, 2, 1, 3]

def columns(parts):
    at, out = 0, {}
    for name, n in parts:
        out[name] = (at, n)
        at += n
    return out, at


C1, C1_N = columns([
    ("ones_d", P), ("head_mean", P), ("rot1", P), ("ident", P), ("iota", P), ("iota16", TOPK),
    ("cos1", 2 * T), ("sin1", 2 * T), ("swa_mask", 2 * T), ("na_mask", 2 * T), ("eps", 1)]
    + [(f"{n}{l}", w) for l in range(DEPTH) for n, w in (
        ("g_mix", KD), ("g_ffn", KD), ("g_qk", 4), ("gate_bias", N_GATE), ("sink", GQA_HEADS),
        ("sub_keys", 2 * KEYS))])
C2, C2_N = columns([
    ("ones_c", P), ("rot2", P), ("cos2", 2 * T), ("sin2", 2 * T), ("dft_d", 2 * P), ("dft_n", 2 * TT * T),
    ("pool", len(POOL_WINDOWS) * TT * T), ("cond", 2 * KD)]
    + [(f"{n}{l}", w) for l in range(DEPTH) for n, w in (
        ("b_mod", N_MOD), ("g1", KD), ("g2", KD), ("g_q", 1), ("g_k", 1), ("dw_w", 2 * CONV), ("dw_b", 2),
        ("ln_g", 2), ("ln_b", 2), ("pool_scale", 2))])

TILES_MIX1 = (N_QK1 + N_V1 + N_GATE) * KD + 2 * KD * 4 + KD * KD + HALVES * KD
TILES_PEER = 2 * KEYS * KD
TILES_L2 = N_MOD * KD + (N_FM2 + N_TM2) * KD + 4 + 4 + 2 + KD * KD + 2 * KF * KD + KD * KF


def blocks(tiles):
    return -(-tiles // BT)


BLOCKS_L1 = blocks(TILES_MIX1) + TILES_PEER // BT
N_BLOCKS = -(-(DEPTH * BLOCKS_L1 + blocks(DEPTH * TILES_L2)) // RING) * RING

TOK_STEP = 16
EXP_STEP = 4


def item_table():
    at, table = 0, {}

    def add(name, n=1):
        nonlocal at
        table.setdefault(name, []).extend(range(at, at + n))
        at += n

    def attention(name, units):
        for u in range(min(2, units)):
            add(name + "S")
        for u in range(units):
            add(name + "T")
            if u + 2 < units:
                add(name + "S")
            add(name + "O")

    for l in range(DEPTH):
        for name, n in (("norm", 1), ("qk", 7), ("val", 5), ("headnorm", 7), ("gate", 8), ("rot", 3)):
            add(f"{name}{l}", n)
        attention(f"att{l}", 16)
        add(f"branch{l}", 8)
        for name, n in (("out", 4), ("fnorm", 1), ("query", 8), ("score", 8), ("route", 2),
                        ("hot", T // 4), ("down", KEYS), ("up", 4)):
            add(f"{name}{l}", n)
    for l in range(DEPTH):
        for name, n in (("mod", 1), ("norm2_", 1), ("fm", 9), ("tm", 3), ("hn2_", 3), ("rot2_", 2)):
            add(f"{name}{l}", n)
        if l == 0:
            attention(f"attc{l}", 4)
        attention(f"attx{l}", 8)
        streams = 2 if l == 0 else 1
        for name, n in (("dft", 3 * streams), ("four", 2), ("pool", 2 * streams), ("plin", 2),
                        ("mean", 1), ("var", 1), ("pw", 2), ("out2_", 8), ("fnorm2_", 1),
                        ("ffn", 2 * KF), ("ffo", 8)):
            add(f"{name}{l}", n)
    return table


ITEMS = item_table()


def attention_order(units):
    steps = [("S", u) for u in range(min(2, units))]
    for u in range(units):
        steps.append(("T", u))
        if u + 2 < units:
            steps.append(("S", u + 2))
        steps.append(("O", u))
    return steps


def program(nc, stream, consts1, consts2, x_in, ctx_in, na_bias, out):
    ctx = ExitStack()
    with ctx:
        def sb(name, shape, dt=FP32):
            return ctx.enter_context(nc.sbuf_tensor(name, shape, dt))

        ring = sb("ring", [P, RING, BT, P])
        x1 = sb("x1", [P, KD, T])
        h1 = sb("h1", [P, KD, T])
        c1 = sb("c1", [P, C1_N])
        route_t = sb("route_t", [P, 3, T])
        route_now = sb("route_now", [P, 3, TOK_STEP])
        small = sb("small", [P, 4 * 512])
        zero_w = sb("zero_w", [P, P])
        mx = sb("mx", [P, 3, 2])
        neg_mx = sb("neg_mx", [P, 3, 2])
        total = sb("total", [P, 3, 2])
        sink_e = sb("sink_e", [P, 3, 2])
        arena = sb("arena", [P, KEYS * T])
        work = [ctx.enter_context(nc.psum_tensor(f"work{b}", [P, 512], FP32)) for b in range(4)]
        acc = [ctx.enter_context(nc.psum_tensor(f"acc{b}", [P, 512], FP32)) for b in range(4)]

        def hot_a(s):
            return small[:, 2 * s * P:(2 * s + 1) * P]

        def hot_b(s):
            return small[:, (2 * s + 1) * P:(2 * s + 2) * P]

        def exp_g(e):
            return small[:, e * T:(e + 1) * T]

        def exp_w(e):
            return small[:, (EXP_STEP + e) * T:(EXP_STEP + e + 1) * T]

        used = [0]

        def carve(*shape):
            n = math.prod(shape)
            view = arena[:, used[0]:used[0] + n]
            used[0] += n
            assert used[0] <= KEYS * T, used[0]
            if len(shape) == 2:
                return view.rearrange("p (a b) -> p a b", b=shape[1])
            if len(shape) == 3:
                return view.rearrange("p (a b c) -> p a b c", b=shape[1], c=shape[2])
            return view

        raw1 = carve(14, T)
        sq1 = carve(7, 2 * T)
        rs1 = carve(7, 2 * T)
        qk1 = carve(14, T)
        rtmp = carve(2 * T)
        v1 = carve(TT, N_V1 * P)
        gates = carve(N_GATE, T)
        bias1 = carve(NA_HEADS, 2 * T)
        prob = carve(3, 2 * T)
        prob_t = carve(2, 2 * T)
        o1 = carve(8, T)
        merged = carve(KD, T)
        mtmp = carve(2, 2 * T)
        rnorm = carve(2 * T)
        used[0] = 0
        qp = carve(HALVES, T)
        sc = carve(TT, HALVES, KEYS)
        sc_rest = carve(KEYS)
        sv = carve(TT, HALVES, TOPK)
        si_f = carve(TT, HALVES, TOPK)
        cand = carve(TOPK, TOPK)
        cand_rest = carve(TOPK * TOPK)
        top = carve(TT, PEER_HEADS * TOPK)
        eq = carve(PEER_HEADS * TOPK, TOPK)
        pick = carve(PEER_HEADS * TOPK, TOPK)
        a_f = carve(PEER_HEADS * TOPK)
        b_f = carve(PEER_HEADS * TOPK)
        routed = carve(TT, 3, P)
        expd = carve(TT, P)
        ssum = carve(TT, PEER_HEADS)
        si = carve(TT, HALVES, TOPK).bitcast(U32)
        sel = carve(TT, PEER_HEADS * TOPK).bitcast(U32)
        a_i = carve(PEER_HEADS * TOPK).bitcast(U32)
        b_i = carve(PEER_HEADS * TOPK).bitcast(U32)
        rnorm_f = carve(T)
        G = arena[:, :].rearrange("p (i t) -> p i t", t=T)
        y_tok = arena[:, 0:TT * D].rearrange("p (a n) -> p a n", n=D)
        used[0] = TT * D
        x2 = carve(KD, 2 * T)
        h2 = carve(KD, 2 * T)
        c2 = carve(C2_N)
        mod = carve(N_MOD, 2)
        gs1 = carve(KD, 2)
        gs2 = carve(KD, 2)
        sc_t = carve(KD, 2)
        rnorm2 = carve(2 * T)
        silu_a = carve(2, 2 * T)
        glu = carve(2, 2, T + 2 * CONV_PAD)
        mark = used[0]
        raw2 = carve(3, 2 * T)
        sq2 = carve(3, 2 * T)
        rs2 = carve(3, 2 * T)
        rtmp2 = carve(2 * T)
        v2 = carve(2 * TT, P)
        p2 = carve(2 * TT, 2 * P)
        f2 = carve(2, 2 * T)
        ca = carve(2, 2 * T)
        cv = carve(2, 2 * T)
        prob2 = carve(3, 2 * T)
        prob2_t = carve(2, 2 * T)
        used_mix = used[0]
        used[0] = mark
        hid = carve(KF, 2 * T)
        used[0] = max(used_mix, used[0])
        mixed = x1[:, :, :].rearrange("p k t -> p (k t)")
        mix_lo = mixed.rearrange("p (k t) -> p k t", t=2 * T)
        mix_hi = h1[:, :, :].rearrange("p k t -> p (k t)").rearrange("p (k t) -> p k t", t=2 * T)
        csq = small[:, 0:4 * T].rearrange("p (a b) -> p a b", b=2 * T)
        ab = small[:, 0:4 * T].rearrange("p (a b) -> p a b", b=2 * T)
        zp = small[:, 4 * T:8 * T].rearrange("p (a b) -> p a b", b=2 * T)
        yf = y_tok[:, 0, :].rearrange("p (a b) -> p a b", b=2 * T)
        cs = y_tok[:, 1, :].rearrange("p (a b) -> p a b", b=2 * T)

        def k1(name, l=""):
            at, n = C1[f"{name}{l}"]
            return c1[:, at:at + n]

        def k2(name, l=""):
            at, n = C2[f"{name}{l}"]
            return c2[:, at:at + n]

        sems = {}

        def sem(name):
            if name not in sems:
                sems[name] = ctx.enter_context(nc.semaphore(name))
            return sems[name]

        block_full = [sem(f"block_full{s}") for s in range(RING)]
        block_free = [sem(f"block_free{s}") for s in range(RING)]
        bank_full = sem("bank_full")
        bank_free = [sem(f"bank_free{b}") for b in range(4)]

        def copied(eng, name, j):
            m = ITEMS[name][j]
            eng.wait_ge(bank_free[m % 4], m // 4 + 1)

        class Steps:

            def __init__(self, eng, name):
                self.eng, self.own, self.n = eng, f"{name}_step", {}

            def step(self, ins, name=None, last=True):
                name = name or self.own
                self.n[name] = self.n.get(name, 0) + 1
                ins.then_inc(sem(name), 1)
                if last:
                    self.eng.wait_ge(sem(name), self.n[name])

            def need(self, name, n):
                self.eng.wait_ge(sem(name), n)

            def full(self, name, j=0):
                m = ITEMS[name][j]
                self.eng.wait_ge(bank_full, m + 1)
                return work[m % 4]

            def free(self, ins, name, j=0):
                m = ITEMS[name][j]
                ins.then_inc(bank_free[m % 4], 1)
                self.eng.wait_ge(bank_free[m % 4], m // 4 + 1)

        block = ctx.enter_context(nc.Block())

        def units1(l):
            out_ = []
            for h in range(NA_HEADS + GQA_HEADS):
                base = HD * (h % 2)
                r = slice(base, base + HD)
                na = h < NA_HEADS
                q = qk1[r, h // 2 if na else 8 + (h - NA_HEADS) // 2, :]
                k = qk1[r, 4 + h // 2 if na else 12, :]
                v0 = h * HD if na else NA_HEADS * HD + base
                out_.append(dict(q=[q[:, 0:P], q[:, P:T]], k=k, nk=T,
                                 v=[v1[:, t, v0:v0 + HD] for t in range(TT)],
                                 bias=bias1[:, h, :] if na else k1("swa_mask"),
                                 sink=None if na else k1("sink", l)[:, h - NA_HEADS:h - NA_HEADS + 1],
                                 o=o1[r, h // 2, :], base=base))
            return out_

        def units2(x_side):
            out_ = []
            for s in range(4):
                base = HD * (s % 2)
                r = slice(base, base + HD)
                vs = [v2[:, t, base:base + HD] for t in range(2 * TT)]
                if not x_side:
                    out_.append(dict(q=[raw2[r, s // 2, t * P:(t + 1) * P] for t in range(TT)],
                                     k=raw2[r, 2, 0:T], nk=T, v=vs[:TT], bias=None, sink=None,
                                     o=mix_lo[r, s // 2, 0:T], base=base))
                    continue
                for t in range(TT):
                    c = T + t * P
                    out_.append(dict(q=[raw2[r, s // 2, c:c + P]], k=raw2[r, 2, :], nk=2 * T, v=vs,
                                     bias=None, sink=None, o=mix_lo[r, s // 2, c:c + P], base=base))
            return out_

        def mix2(n):
            return mix_lo[:, n, :] if n < 4 else mix_hi[:, n - 4, :]

        @block.sync
        def _(sp):
            sp.dma_start(x1[:, :, :], x_in.rearrange("k p t -> p k t")).then_inc(sem("x_loaded"), 16)
            for s in range(RING):
                sp.dma_start(ring[:, s, :, :].rearrange("p a b -> p (a b)"), stream[s, :, :])\
                  .then_inc(block_full[s], 16)
            with sp.Fori(1, N_BLOCKS // RING) as i:
                for s in range(RING):
                    sp.wait_ge(block_free[s], i)
                    sp.dma_start(ring[:, s, :, :].rearrange("p a b -> p (a b)"),
                                 stream[bass.ds(i * RING + s, 1), :, :].rearrange("a p n -> p (a n)"))\
                      .then_inc(block_full[s], 16)
            copied(sp, f"ffo{DEPTH - 1}", KD - 1)
            sp.dma_start(out.rearrange("k p t -> p k t"), x2[:, :, T:2 * T]).then_inc(sem("stored"), 16)
            sp.wait_ge(sem("stored"), 16)

        @block.gpsimd
        def _(pool):
            pool.dma_start(c1[:, :], consts1[:, :]).then_inc(sem("c1_loaded"), 16)
            for l in range(DEPTH):
                if l:
                    copied(pool, f"up{l - 1}", 3)
                pool.dma_start(bias1[:, :, :].rearrange("p a b -> p (a b)"), na_bias[l, :, :])\
                    .then_inc(sem("bias_loaded"), 16)
            copied(pool, f"up{DEPTH - 1}", 3)
            pool.dma_start(c2[:, :], consts2[:, :]).then_inc(sem("c2_loaded"), 16)
            pool.dma_start(x2[:, :, 0:T], ctx_in.rearrange("k p t -> p k t")).then_inc(sem("ctx_loaded"), 16)
            pool.memset(glu[:, :, :, :], 0.0).then_inc(sem("glu_zero"), 1)

        @block.tensor
        def _(pe):
            at = [0]
            owed = []

            def mm(o, w, r, start=True, stop=True, inc=None, **kw):
                ins = nc.tensor.matmul(o, w, r, start=start, stop=stop, **kw)
                if inc is not None:
                    ins.then_inc(inc, 1)
                elif owed:
                    ins.then_inc(owed.pop(0), 1)
                return ins

            def tile():
                b, j = divmod(at[0], BT)
                if j == 0:
                    pe.wait_ge(block_full[b % RING], 16 * (b // RING + 1))
                at[0] += 1
                return ring[:, b % RING, j, :]

            def read(n=1):
                for end in range(at[0] - n + 1, at[0] + 1):
                    if end % BT == 0:
                        owed.append(block_free[(end // BT - 1) % RING])

            def bank(name, j=0):
                m = ITEMS[name][j]
                if m >= 4:
                    pe.wait_ge(bank_free[m % 4], m // 4)
                return work[m % 4]

            def group(o, n_k, rhs, last, first=None):
                for k in range(n_k):
                    w = tile()
                    if first:
                        pe.wait_ge(sem(first[0]), first[1] * (k + 1))
                    read_inc = last and k == n_k - 1
                    mm(o, w, rhs(k), k == 0, k == n_k - 1, inc=bank_full if read_inc else None)
                    read()

            def pairs(name, n_tiles, n_k, rhs, first=None):
                for j in range(-(-n_tiles // 2)):
                    b = bank(name, j)
                    m = min(2, n_tiles - 2 * j)
                    for a in range(m):
                        for k in range(n_k):
                            if first and j == 0 and a == 0:
                                pe.wait_ge(sem(first), k + 1)
                            mm(b[:, a * T:(a + 1) * T], tile(), rhs(k), k == 0, k == n_k - 1,
                               inc=bank_full if (a == m - 1 and k == n_k - 1) else None)
                            read()

            def square_sum(name, ready, ones, src, n_k, cols):
                b = bank(name)
                pe.wait_ge(sem(ready), 1)
                for k in range(n_k):
                    mm(b[:, 0:cols], ones, src(k), k == 0, k == n_k - 1,
                       inc=bank_full if k == n_k - 1 else None)

            def transpose_to(o, src, ident, inc=None):
                ins = nc.tensor.transpose(o, src, ident)
                if inc is not None:
                    ins.then_inc(inc, 1)

            def attention(name, units, prob_, prob_t_, ready):
                pe.wait_ge(sem(ready[0]), ready[1])
                copied(pe, *ready[2:])
                for kind, u in attention_order(len(units)):
                    un = units[u]
                    b = bank(f"{name}{kind}", u)
                    nq, nk = len(un["q"]), un["nk"]
                    if kind == "S":
                        for g in range(nq):
                            mm(b[:, g * nk:(g + 1) * nk], un["q"][g], un["k"],
                               inc=bank_full if g == nq - 1 else None)
                    elif kind == "T":
                        pe.wait_ge(sem(f"{name}_prob"), u + 1)
                        for g in range(nq):
                            for kt in range(nk // P):
                                transpose_to(b[:, (kt * nq + g) * P:(kt * nq + g + 1) * P],
                                             prob_[:, u % 3, g * nk + kt * P:g * nk + (kt + 1) * P],
                                             k1("ident"),
                                             bank_full if (g == nq - 1 and kt == nk // P - 1) else None)
                    else:
                        copied(pe, f"{name}T", u)
                        base = un["base"]
                        for kt in range(nk // P):
                            mm(b[base:base + HD, 0:nq * P], un["v"][kt],
                               prob_t_[:, u % 2, kt * nq * P:(kt + 1) * nq * P],
                               kt == 0, kt == nk // P - 1, inc=bank_full if kt == nk // P - 1 else None)

            pe.wait_ge(sem("c1_loaded"), 16)
            for l in range(DEPTH):
                square_sum(f"norm{l}", f"sq_mix{l}", k1("ones_d"), lambda k: h1[:, k, :], KD, T)
                pairs(f"qk{l}", N_QK1, KD, lambda k: h1[:, k, :], first=f"h_mix{l}")
                for n in range(N_V1):
                    b = bank(f"val{l}", n)
                    ws = [tile() for _ in range(KD)]
                    for t in range(TT):
                        for k in range(KD):
                            mm(b[:, t * P:(t + 1) * P], h1[:, k, t * P:(t + 1) * P], ws[k],
                               k == 0, k == KD - 1,
                               inc=bank_full if (t == TT - 1 and k == KD - 1) else None)
                    read(KD)
                for j in range(7):
                    w = 2 * T if j < 6 else T
                    b = bank(f"headnorm{l}", j)
                    pe.wait_ge(sem(f"sq_head{l}"), j + 1)
                    mm(b[:, 0:w], k1("head_mean"), sq1[:, j, 0:w], inc=bank_full)
                pairs(f"gate{l}", N_GATE, KD, lambda k: h1[:, k, :])
                for j in range(3):
                    w = 2 * T if j < 2 else T
                    b = bank(f"rot{l}", j)
                    pe.wait_ge(sem(f"qk_normed{l}"), 5 + j)
                    src = qk1[:, 8 + 2 * j:10 + 2 * j, :].rearrange("p a b -> p (a b)")
                    mm(b[:, 0:w], k1("rot1"), src[:, 0:w], inc=bank_full)
                attention(f"att{l}", units1(l), prob, prob_t, (f"rotated{l}", 3, f"val{l}", N_V1 - 1))
                copied(pe, f"att{l}O", 15)
                for j in range(4):
                    for half in range(2):
                        b = bank(f"branch{l}", 2 * j + half)
                        for a in range(2):
                            group(b[:, a * T:(a + 1) * T], 4, lambda k: o1[:, 4 * half + k, :], a == 1)
                pe.wait_ge(sem(f"merged{l}"), 4)
                pairs(f"out{l}", KD, KD, lambda k: merged[:, k, :])
                square_sum(f"fnorm{l}", f"sq_ffn{l}", k1("ones_d"), lambda k: h1[:, k, :], KD, T)
                pairs(f"query{l}", HALVES, KD, lambda k: h1[:, k, :], first=f"h_ffn{l}")
                sk = k1("sub_keys", l)
                for j in range(8):
                    t, quad = divmod(j, 4)
                    b = bank(f"score{l}", j)
                    copied(pe, f"query{l}", 2 * quad + 1)
                    for a in range(4):
                        hp = 4 * quad + a
                        mm(b[:, a * KEYS:(a + 1) * KEYS], qp[:, hp, t * P:(t + 1) * P],
                           sk[:, (hp % 2) * KEYS:(hp % 2 + 1) * KEYS], inc=bank_full if a == 3 else None)
                for t in range(TT):
                    b = bank(f"route{l}", t)
                    pe.wait_ge(sem(f"routed{l}"), t + 1)
                    for a in range(3):
                        transpose_to(b[:, a * P:(a + 1) * P], routed[:, t, a, :], k1("ident"),
                                     bank_full if a == 2 else None)
                base = ITEMS[f"hot{l}"][0]
                assert not owed
                with pe.Fori(0, T // TOK_STEP) as i:
                    for q in range(TOK_STEP // 4):
                        m = base + q
                        pe.wait_ge(bank_free[m % 4], i * (TOK_STEP // 16) + m // 4)
                        for u in range(4):
                            s = 4 * (q % 2) + u
                            pe.wait_ge(sem(f"hot{l}"), i * TOK_STEP + 4 * q + u + 1)
                            mm(work[m % 4][:, u * P:(u + 1) * P], hot_b(s), hot_a(s),
                               inc=bank_full if u == 3 else None)
                if at[0] % BT:
                    owed.append(block_free[(at[0] // BT) % RING])
                    at[0] += BT - at[0] % BT
                b0 = at[0] // BT
                base = ITEMS[f"down{l}"][0]
                pe.wait_ge(sem("zeroed"), 1)
                for a in range(4):
                    mm(acc[a][:, :], zero_w[:, :], k1("cos1"), True, False, skip_group_check=True)
                assert not owed
                with pe.Fori(0, KEYS // EXP_STEP) as i:
                    for pair in range(EXP_STEP // 2):
                        bu, bv = b0 + 2 * pair, b0 + 2 * pair + 1
                        pe.wait_ge(block_full[bu % RING], i * 16 + 16 * (bu // RING + 1))
                        for e in range(2):
                            m = base + 2 * pair + e
                            pe.wait_ge(bank_free[m % 4], i + m // 4)
                            for k in range(KD):
                                mm(work[m % 4][:, 0:T], ring[:, bu % RING, e * KD + k, :], h1[:, k, :],
                                   k == 0, k == KD - 1, inc=bank_full if k == KD - 1 else None)
                        pe.wait_ge(block_full[bv % RING], i * 16 + 16 * (bv // RING + 1))
                        owed.append(block_free[bu % RING])
                        for e in range(2):
                            ei = 2 * pair + e
                            pe.wait_ge(sem(f"weighted{l}"), i * EXP_STEP + ei + 1)
                            for t in range(TT):
                                for n in range(2):
                                    end = e == 1 and t == 1 and n == 1
                                    mm(acc[2 * t + n][:, :], exp_w(ei)[:, t * P:(t + 1) * P],
                                       ring[:, bv % RING, e * KD + 4 * n:e * KD + 4 * n + 4, :]
                                       .rearrange("p a b -> p (a b)"), False, False,
                                       inc=block_free[bv % RING] if end else None, skip_group_check=True)
                for a in range(4):
                    mm(acc[a][:, :], zero_w[:, :], k1("cos1"), False, True, skip_group_check=True,
                       inc=sem(f"up{l}"))
                at[0] += TILES_PEER
                pe.wait_ge(sem(f"y_copied{l}"), 4)
                for j in range(4):
                    b = bank(f"up{l}", j)
                    for a in range(2):
                        for t in range(TT):
                            n = 2 * j + a
                            transpose_to(b[:, a * T + t * P:a * T + (t + 1) * P],
                                         y_tok[:, t, n * P:(n + 1) * P], k1("ident"),
                                         bank_full if (a == 1 and t == TT - 1) else None)

            pe.wait_ge(sem("c2_loaded"), 16)
            for l in range(DEPTH):
                lo = 0 if l == 0 else T
                n_c = 2 * T - lo
                b = bank(f"mod{l}")
                pe.wait_ge(sem("cond_silu"), 1)
                for n in range(N_MOD):
                    group(b[:, 2 * n:2 * n + 2], KD, lambda k: sc_t[:, k, :], n == N_MOD - 1)
                square_sum(f"norm2_{l}", f"sq2_{l}", k1("ones_d"), lambda k: h2[:, k, :], KD, 2 * T)
                for n in range(N_FM2):
                    c = 0 if n == 2 else lo
                    b = bank(f"fm{l}", n)
                    group(b[:, c:2 * T], KD, lambda k: h2[:, k, c:2 * T], True,
                          (f"h2_{l}", 2) if n == 0 else None)
                for n in range(N_TM2):
                    b = bank(f"tm{l}", n)
                    ws = [tile() for _ in range(KD)]
                    ts = list(range(0 if n == 0 else lo // P, 2 * TT))
                    for t in ts:
                        for k in range(KD):
                            mm(b[:, t * P:(t + 1) * P], h2[:, k, t * P:(t + 1) * P], ws[k],
                               k == 0, k == KD - 1, inc=bank_full if (t == ts[-1] and k == KD - 1) else None)
                    read(KD)
                for j in range(3):
                    c = 0 if j == 2 else lo
                    b = bank(f"hn2_{l}", j)
                    pe.wait_ge(sem(f"sq_head2_{l}"), j + 1)
                    mm(b[:, c:2 * T], k1("head_mean"), sq2[:, j, c:2 * T], inc=bank_full)
                for j in range(2):
                    b = bank(f"rot2_{l}", j)
                    pe.wait_ge(sem(f"qk_normed2_{l}"), 2 + j)
                    for a in range(2 - j):
                        mm(b[:, a * T:(a + 1) * T], k2("rot2"), raw2[:, 2 * j + a, T:2 * T],
                           inc=bank_full if a == 1 - j else None)
                if l == 0:
                    attention(f"attc{l}", units2(False), prob2, prob2_t,
                              (f"rotated2_{l}", 2, f"tm{l}", 0))
                attention(f"attx{l}", units2(True), prob2, prob2_t, (f"rotated2_{l}", 2, f"tm{l}", 0))
                copied(pe, f"fm{l}", 4)
                dn = k2("dft_n")
                for s in range(lo // T, 2):
                    i0 = 3 * (s - lo // T)
                    for t in range(TT):
                        b = bank(f"dft{l}", i0 + t)
                        for a in range(2):
                            mm(b[:, a * T:(a + 1) * T], f2[:, a, s * T + t * P:s * T + (t + 1) * P],
                               k2("dft_d"), inc=bank_full if a == 1 else None)
                    b = bank(f"dft{l}", i0 + 2)
                    copied(pe, f"dft{l}", i0 + 1)
                    for a in range(2):
                        for t in range(TT):
                            for part in range(2):
                                c = (2 * t + part) * T
                                mm(b[:, a * T:(a + 1) * T],
                                   ab[:, t, (2 * a + part) * P:(2 * a + part + 1) * P], dn[:, c:c + T],
                                   t + part == 0, t + part == 2,
                                   inc=bank_full if a + t + part == 3 else None)
                copied(pe, f"dft{l}", 3 * (n_c // T) - 1)
                for n in range(2):
                    b = bank(f"four{l}", n)
                    group(b[:, lo:2 * T], 2, lambda k: yf[:, k, lo:2 * T], True)
                copied(pe, f"tm{l}", 2)
                pm = k2("pool")
                for s in range(lo // T, 2):
                    for c in range(2):
                        b = bank(f"pool{l}", 2 * (s - lo // T) + c)
                        for a in range(2):
                            for t in range(TT):
                                o = ((2 * c + a) * TT + t) * T
                                mm(b[:, a * T:(a + 1) * T], p2[:, s * TT + t, c * P:(c + 1) * P],
                                   pm[:, o:o + T], t == 0, t == TT - 1,
                                   inc=bank_full if a + t == 2 else None)
                for c in range(2):
                    b = bank(f"plin{l}", c)
                    copied(pe, f"pool{l}", 2 * (n_c // T) - 1)
                    group(b[:, lo:2 * T], 1, lambda k: zp[:, c, lo:2 * T], True)
                b = bank(f"mean{l}")
                pe.wait_ge(sem(f"conv{l}"), 2)
                for k in range(2):
                    mm(b[:, lo:2 * T], k2("ones_c"), cv[:, k, lo:2 * T], k == 0, k == 1,
                       inc=bank_full if k else None)
                b = bank(f"var{l}")
                pe.wait_ge(sem(f"csq{l}"), 2)
                for k in range(2):
                    mm(b[:, lo:2 * T], k2("ones_c"), csq[:, k, lo:2 * T], k == 0, k == 1,
                       inc=bank_full if k else None)
                pe.wait_ge(sem(f"cs{l}"), 2)
                for n in range(2):
                    b = bank(f"pw{l}", n)
                    group(b[:, lo:2 * T], 2, lambda k: cs[:, k, lo:2 * T], True)
                copied(pe, f"pw{l}", 1)
                for n in range(KD):
                    b = bank(f"out2_{l}", n)
                    group(b[:, lo:2 * T], KD, lambda k: mix2(k)[:, lo:2 * T], True)
                square_sum(f"fnorm2_{l}", f"sqf2_{l}", k1("ones_d"), lambda k: h2[:, k, lo:2 * T], KD, n_c)
                for j in range(2 * KF):
                    b = bank(f"ffn{l}", j)
                    group(b[:, lo:2 * T], KD, lambda k: h2[:, k, lo:2 * T], True,
                          (f"hf2_{l}", n_c // T) if j == 0 else None)
                for n in range(KD):
                    b = bank(f"ffo{l}", n)
                    for k in range(KF):
                        if n == 0:
                            copied(pe, f"ffn{l}", 2 * k + 1)
                        mm(b[:, lo:2 * T], tile(), hid[:, k, lo:2 * T], k == 0, k == KF - 1,
                           inc=bank_full if k == KF - 1 else None)
                        read()
            at_end = N_BLOCKS // RING * 16
            for s in range(RING):
                pe.wait_ge(block_full[s], at_end)

        def flat(ap):
            return ap.rearrange("p a b -> p (a b)")

        @block.scalar
        def _(act):
            A = Steps(act, "act")
            f = nc.scalar.activation

            def attention(name, units, prob_, prob_t_):
                def exps(u):
                    un = units[u]
                    nq, nk, s = len(un["q"]), un["nk"], u % 3
                    A.need(f"{name}_score", u + 1)
                    if un["sink"] is not None:
                        for g in range(nq):
                            A.step(f(sink_e[:, s, g:g + 1], un["sink"], ACT.Exp, bias=neg_mx[:, s, g:g + 1]))
                    for g in range(nq):
                        c = prob_[:, s, g * nk:(g + 1) * nk]
                        A.step(f(c, c, ACT.Exp, bias=neg_mx[:, s, g:g + 1], accum_out=total[:, s, g:g + 1]),
                               f"{name}_exp")
                exps(0)
                for u, un in enumerate(units):
                    if u + 1 < len(units):
                        exps(u + 1)
                    base, nq = un["base"], len(un["q"])
                    b = A.full(f"{name}T", u)
                    A.free(f(prob_t_[:, u % 2, :], b[:, :], ACT.Copy), f"{name}T", u)
                    b = A.full(f"{name}O", u)
                    A.free(f(un["o"], b[base:base + HD, 0:nq * P], ACT.Copy), f"{name}O", u)

            A.need("c1_loaded", 16)
            A.need("x_loaded", 16)
            for l in range(DEPTH):
                if l:
                    copied(act, f"up{l - 1}", 3)
                A.step(f(flat(h1[:, :, :]), flat(x1[:, :, :]), ACT.Square), f"sq_mix{l}")
                b = A.full(f"norm{l}")
                A.free(f(rnorm[:, 0:T], b[:, 0:T], ACT.Sqrt, bias=k1("eps")), f"norm{l}")
                for j in range(7):
                    w = 2 * T if j < 6 else T
                    b = A.full(f"qk{l}", j)
                    raw = flat(raw1[:, 2 * j:2 * j + 2, :])[:, 0:w]
                    A.free(f(raw, b[:, 0:w], ACT.Copy), f"qk{l}", j)
                    A.step(f(sq1[:, j, 0:w], raw, ACT.Square), f"sq_head{l}")
                for n in range(N_V1):
                    b = A.full(f"val{l}", n)
                    A.free(f(v1[:, :, n * P:(n + 1) * P], b[:, 0:T].rearrange("p (a b) -> p a b", b=P), ACT.Copy),
                           f"val{l}", n)
                for j in range(7):
                    w = 2 * T if j < 6 else T
                    b = A.full(f"headnorm{l}", j)
                    A.free(f(rs1[:, j, 0:w], b[:, 0:w], ACT.Sqrt, bias=k1("eps")), f"headnorm{l}", j)
                for j in range(8):
                    b = A.full(f"gate{l}", j)
                    for a in range(2):
                        n = 2 * j + a
                        ins = f(gates[:, n, :], b[:, a * T:(a + 1) * T], ACT.Sigmoid,
                                bias=k1("gate_bias", l)[:, n:n + 1])
                        if a:
                            A.free(ins, f"gate{l}", j)
                attention(f"att{l}", units1(l), prob, prob_t)
                copied(act, f"out{l}", 3)
                A.step(f(flat(h1[:, :, :]), flat(x1[:, :, :]), ACT.Square), f"sq_ffn{l}")
                b = A.full(f"fnorm{l}")
                A.free(f(rnorm_f, b[:, 0:T], ACT.Sqrt, bias=k1("eps")), f"fnorm{l}")
                for j in range(8):
                    b = A.full(f"query{l}", j)
                    A.free(f(flat(qp[:, 2 * j:2 * j + 2, :]), b[:, :], ACT.Copy), f"query{l}", j)
                for j in range(8):
                    t, quad = divmod(j, 4)
                    b = A.full(f"score{l}", j)
                    A.free(f(flat(sc[:, t, 4 * quad:4 * quad + 4, :]), b[:, :], ACT.Copy), f"score{l}", j)
                for t in range(TT):
                    A.need(f"logit{l}", t + 1)
                    A.step(f(expd[:, t, :], expd[:, t, :], ACT.Exp), f"expd{l}")
                for t in range(TT):
                    b = A.full(f"route{l}", t)
                    A.free(f(route_t[:, :, t * P:(t + 1) * P],
                             b[:, 0:3 * P].rearrange("p (a b) -> p a b", b=P), ACT.Copy), f"route{l}", t)
                base = ITEMS[f"hot{l}"][0]
                with act.Fori(0, T // TOK_STEP) as i:
                    for q in range(TOK_STEP // 4):
                        m = base + q
                        act.wait_ge(bank_full, i * (TOK_STEP // 4) + m + 1)
                        f(G[:, :, bass.ds(i * TOK_STEP + 4 * q, 4)],
                          work[m % 4][:, :].rearrange("p (t i) -> p i t", i=KEYS), ACT.Copy)\
                            .then_inc(bank_free[m % 4], 1)
                copied(act, f"hot{l}", T // 4 - 1)
                base = ITEMS[f"down{l}"][0]
                with act.Fori(0, KEYS // EXP_STEP) as i:
                    for e in range(EXP_STEP):
                        m = base + e
                        act.wait_ge(bank_full, i * EXP_STEP + m + 1)
                        f(exp_g(e), work[m % 4][:, 0:T], ACT.Gelu).then_inc(bank_free[m % 4], 1)
                for a in range(4):
                    A.need(f"up{l}", a + 1)
                    A.step(f(y_tok[:, a // 2, (a % 2) * 512:(a % 2 + 1) * 512], acc[a][:, :], ACT.Copy),
                           f"y_copied{l}")

            A.need("c2_loaded", 16)
            A.step(f(flat(sc_t[:, :, :]), k2("cond"), ACT.Silu), "cond_silu")
            A.need("ctx_loaded", 16)
            A.need("x_copied", 1)
            for l in range(DEPTH):
                lo = 0 if l == 0 else T
                cols = [slice(s * T, (s + 1) * T) for s in range(2)]
                if l:
                    copied(act, f"ffo{l - 1}", KD - 1)
                A.step(f(flat(h2[:, :, :]), flat(x2[:, :, :]), ACT.Square), f"sq2_{l}")
                b = A.full(f"norm2_{l}")
                A.free(f(rnorm2, b[:, :], ACT.Sqrt, bias=k1("eps")), f"norm2_{l}")

                def shift(scaled, done, chunk, s0):
                    for k in range(KD):
                        for s in range(s0, 2):
                            A.need(scaled, k * (2 - s0) + s - s0 + 1)
                            c = h2[:, k, cols[s]]
                            A.step(f(c, c, ACT.Identity, bias=mod[:, chunk * KD + k, s:s + 1]), done, last=False)
                shift(f"hs2_{l}", f"h2_{l}", 0, 0)
                for n in range(N_FM2):
                    c = slice(0 if n == 2 else lo, 2 * T)
                    b = A.full(f"fm{l}", n)
                    if n < 3:
                        A.free(f(raw2[:, n, c], b[:, c], ACT.Copy), f"fm{l}", n)
                        A.step(f(sq2[:, n, c], raw2[:, n, c], ACT.Square), f"sq_head2_{l}")
                    elif n < 5:
                        A.free(f(f2[:, n - 3, c], b[:, c], ACT.Copy), f"fm{l}", n)
                    elif n < 7:
                        A.free(f(ca[:, n - 5, c], b[:, c], ACT.Copy), f"fm{l}", n)
                    else:
                        A.free(f(cv[:, n - 7, c], b[:, c], ACT.Sigmoid), f"fm{l}", n)
                for n in range(N_TM2):
                    t0 = 0 if n == 0 else lo // P
                    b = A.full(f"tm{l}", n)
                    src = b[:, t0 * P:4 * P].rearrange("p (a b) -> p a b", b=P)
                    dst = v2[:, :, :] if n == 0 else p2[:, t0:4, (n - 1) * P:n * P]
                    A.free(f(dst, src, ACT.Copy), f"tm{l}", n)
                for j in range(3):
                    c = slice(0 if j == 2 else lo, 2 * T)
                    b = A.full(f"hn2_{l}", j)
                    A.free(f(rs2[:, j, c], b[:, c], ACT.Sqrt, bias=k1("eps")), f"hn2_{l}", j)
                if l == 0:
                    attention(f"attc{l}", units2(False), prob2, prob2_t)
                attention(f"attx{l}", units2(True), prob2, prob2_t)
                for s in range(lo // T, 2):
                    i0 = 3 * (s - lo // T)
                    for t in range(TT):
                        b = A.full(f"dft{l}", i0 + t)
                        A.free(f(ab[:, t, :], b[:, :], ACT.Copy), f"dft{l}", i0 + t)
                    b = A.full(f"dft{l}", i0 + 2)
                    A.free(f(yf[:, :, cols[s]], b[:, :].rearrange("p (a b) -> p a b", b=T), ACT.Copy),
                           f"dft{l}", i0 + 2)
                c = slice(lo, 2 * T)
                for n in range(2):
                    b = A.full(f"four{l}", n)
                    A.free(f(mix2(2 + n)[:, c], b[:, c], ACT.Copy), f"four{l}", n)
                for s in range(lo // T, 2):
                    for g in range(2):
                        j = 2 * (s - lo // T) + g
                        b = A.full(f"pool{l}", j)
                        f(zp[0:HD, g, cols[s]], b[0:HD, 0:T], ACT.Copy)
                        A.free(f(zp[HD:P, g, cols[s]], b[HD:P, T:2 * T], ACT.Copy), f"pool{l}", j)
                for g in range(2):
                    b = A.full(f"plin{l}", g)
                    A.free(f(mix2(6 + g)[:, c], b[:, c], ACT.Identity, scale=k2("pool_scale", l)[:, g:g + 1]),
                           f"plin{l}", g)
                copied(act, f"mean{l}", 0)
                for g in range(2):
                    A.step(f(csq[:, g, c], cv[:, g, c], ACT.Square), f"csq{l}")
                b = A.full(f"var{l}")
                A.free(f(rnorm2[:, c], b[:, c], ACT.Sqrt, bias=k1("eps")), f"var{l}")
                for g in range(2):
                    A.need(f"conv_normed{l}", g + 1)
                    A.step(f(cs[:, g, c], cv[:, g, c], ACT.Silu, scale=k2("ln_g", l)[:, g:g + 1],
                             bias=k2("ln_b", l)[:, g:g + 1]), f"cs{l}")
                for g in range(2):
                    b = A.full(f"pw{l}", g)
                    A.free(f(mix2(4 + g)[:, c], b[:, c], ACT.Copy), f"pw{l}", g)
                copied(act, f"out2_{l}", KD - 1)
                A.step(f(h2[:, :, c], x2[:, :, c], ACT.Square), f"sqf2_{l}")
                b = A.full(f"fnorm2_{l}")
                A.free(f(rnorm2[:, c], b[:, 0:2 * T - lo], ACT.Sqrt, bias=k1("eps")), f"fnorm2_{l}")
                shift(f"hsf2_{l}", f"hf2_{l}", 3, lo // T)
                for j in range(KF):
                    b = A.full(f"ffn{l}", 2 * j)
                    if j >= 2:
                        copied(act, f"ffn{l}", 2 * (j - 2) + 1)
                    A.free(f(silu_a[:, j % 2, c], b[:, c], ACT.Silu), f"ffn{l}", 2 * j)

        @block.vector
        def _(dve):
            V = Steps(dve, "dve")
            v = nc.vector

            def stt(o, a, s, b, op0=ALU.mult, op1=ALU.mult):
                return v.scalar_tensor_tensor(o, a, s, b, op0, op1)

            def attention(name, units, prob_):
                def score(u):
                    un = units[u]
                    nq, s = len(un["q"]), u % 3
                    b = V.full(f"{name}S", u)
                    if un["bias"] is not None:
                        V.free(stt(prob_[:, s, :], b[:, :], SCALE, un["bias"], ALU.mult, ALU.add), f"{name}S", u)
                    else:
                        V.free(v.tensor_scalar(prob_[:, s, :], b[:, :], SCALE, None, ALU.mult), f"{name}S", u)
                    V.step(v.tensor_reduce(mx[:, s, 0:nq], prob_[:, s, :].rearrange("p (a b) -> p a b", a=nq),
                                           AX.X, ALU.max))
                    if un["sink"] is not None:
                        V.step(v.tensor_scalar(neg_mx[:, s, 0:nq], mx[:, s, 0:nq], un["sink"], -1.0,
                                               ALU.max, ALU.mult), f"{name}_score")
                    else:
                        V.step(v.tensor_scalar(neg_mx[:, s, 0:nq], mx[:, s, 0:nq], -1.0, None, ALU.mult),
                               f"{name}_score")

                def normalise(u):
                    un = units[u]
                    nq, nk, s = len(un["q"]), un["nk"], u % 3
                    V.need(f"{name}_exp", sum(len(units[x]["q"]) for x in range(u + 1)))
                    if un["sink"] is not None:
                        V.step(v.tensor_tensor(total[:, s, 0:nq], total[:, s, 0:nq], sink_e[:, s, 0:nq], ALU.add))
                    V.step(v.reciprocal(total[:, s, 0:nq], total[:, s, 0:nq]))
                    for g in range(nq):
                        c = prob_[:, s, g * nk:(g + 1) * nk]
                        ins = v.tensor_scalar(c, c, total[:, s, g:g + 1], None, ALU.mult)
                        if g == nq - 1:
                            V.step(ins, f"{name}_prob")
                score(0)
                for u in range(len(units)):
                    if u + 1 < len(units):
                        score(u + 1)
                    normalise(u)

            V.step(v.memset(zero_w[:, :], 0.0), "zeroed")
            V.need("c1_loaded", 16)
            for l in range(DEPTH):
                def normalise_features(item, r, g, done):
                    copied(dve, item, 0)
                    V.step(v.reciprocal(r, r))
                    for k in range(KD):
                        V.step(stt(h1[:, k, :], x1[:, k, :], g[:, k:k + 1], r), done, last=False)

                normalise_features(f"norm{l}", rnorm[:, 0:T], k1("g_mix", l), f"h_mix{l}")
                V.need("bias_loaded", 16 * (l + 1))
                for h in range(NA_HEADS):
                    V.step(v.tensor_tensor(bias1[:, h, :], bias1[:, h, :], k1("na_mask"), ALU.add))
                for j in range(7):
                    w = 2 * T if j < 6 else T
                    g = (0, 0, 1, 1, 2, 2, 3)[j]
                    copied(dve, f"headnorm{l}", j)
                    r = rs1[:, j, 0:w]
                    V.step(v.reciprocal(r, r))
                    V.step(stt(flat(qk1[:, 2 * j:2 * j + 2, :])[:, 0:w], flat(raw1[:, 2 * j:2 * j + 2, :])[:, 0:w],
                               k1("g_qk", l)[:, g:g + 1], r), f"qk_normed{l}")
                for j in range(3):
                    w = 2 * T if j < 2 else T
                    b = V.full(f"rot{l}", j)
                    q = flat(qk1[:, 8 + 2 * j:10 + 2 * j, :])[:, 0:w]
                    V.free(v.tensor_tensor(rtmp[:, 0:w], b[:, 0:w], k1("sin1")[:, 0:w], ALU.mult), f"rot{l}", j)
                    V.step(v.tensor_tensor(q, q, k1("cos1")[:, 0:w], ALU.mult))
                    V.step(v.tensor_tensor(q, q, rtmp[:, 0:w], ALU.add), f"rotated{l}")
                attention(f"att{l}", units1(l), prob)
                copied(dve, f"gate{l}", 7)
                for j in range(4):
                    m = flat(merged[:, 2 * j:2 * j + 2, :])
                    b = V.full(f"branch{l}", 2 * j)
                    V.free(v.tensor_tensor(m, b[:, :], flat(gates[:, 2 * j:2 * j + 2, :]), ALU.mult),
                           f"branch{l}", 2 * j)
                    b = V.full(f"branch{l}", 2 * j + 1)
                    V.free(v.tensor_tensor(mtmp[:, 0, :], b[:, :], flat(gates[:, KD + 2 * j:KD + 2 * j + 2, :]),
                                           ALU.mult), f"branch{l}", 2 * j + 1)
                    V.step(v.tensor_tensor(m, m, mtmp[:, 0, :], ALU.add), f"merged{l}")

                def add_to_residual(item):
                    for j in range(4):
                        b = V.full(item, j)
                        c = flat(x1[:, 2 * j:2 * j + 2, :])
                        V.free(v.tensor_tensor(c, b[:, :], c, ALU.add), item, j)

                add_to_residual(f"out{l}")
                normalise_features(f"fnorm{l}", rnorm_f, k1("g_ffn", l), f"h_ffn{l}")

                def top16(values, rest, src, indices):
                    V.step(v.max(values[:, 0:8], src))
                    V.step(v.max_index(indices[:, 0:8], values[:, 0:8], src))
                    V.step(v.match_replace(rest, values[:, 0:8], src, -3.0e38))
                    V.step(v.max(values[:, 8:16], rest))
                    V.step(v.max_index(indices[:, 8:16], values[:, 8:16], rest))

                for t in range(TT):
                    copied(dve, f"score{l}", 4 * t + 3)
                    for hp in range(HALVES):
                        top16(sv[:, t, hp, :], sc_rest, sc[:, t, hp, :], si[:, t, hp, :])
                    V.step(v.tensor_copy(si_f[:, t, :, :], si[:, t, :, :]))
                    for h in range(PEER_HEADS):
                        s0 = sv[:, t, 2 * h, :].unsqueeze(2).broadcast_to([P, TOPK, TOPK])
                        s1 = sv[:, t, 2 * h + 1, :].unsqueeze(1).broadcast_to([P, TOPK, TOPK])
                        V.step(v.tensor_tensor(cand[:, :, :], s0, s1, ALU.add))
                        c = slice(h * TOPK, (h + 1) * TOPK)
                        top16(top[:, t, c], cand_rest, flat(cand[:, :, :]), sel[:, t, c])
                    tv = top[:, t, :].rearrange("p (h k) -> p h k", k=TOPK)
                    ev = expd[:, t, :].rearrange("p (h k) -> p h k", k=TOPK)
                    V.step(v.tensor_tensor(ev, tv, tv[:, :, 0:1].broadcast_to([P, PEER_HEADS, TOPK]),
                                           ALU.subtract), f"logit{l}")
                    V.step(v.tensor_single_scalar(a_i, sel[:, t, :], 4, ALU.logical_shift_right))
                    V.step(v.tensor_single_scalar(b_i, sel[:, t, :], 15, ALU.bitwise_and))
                    V.step(v.tensor_copy(a_f, a_i))
                    V.step(v.tensor_copy(b_f, b_i))
                    slots = PEER_HEADS * TOPK
                    places = k1("iota16").unsqueeze(1).broadcast_to([P, slots, TOPK])
                    for half, place in ((0, a_f), (1, b_f)):
                        V.step(v.tensor_tensor(eq[:, :, :], place.unsqueeze(2).broadcast_to([P, slots, TOPK]),
                                               places, ALU.is_equal))
                        numbers = si_f[:, t, half::2, :].unsqueeze(2).broadcast_to([P, PEER_HEADS, TOPK, TOPK])
                        V.step(v.tensor_tensor(pick[:, :, :].rearrange("p (h k) a -> p h k a", k=TOPK),
                                               eq[:, :, :].rearrange("p (h k) a -> p h k a", k=TOPK),
                                               numbers, ALU.mult))
                        V.step(v.tensor_reduce(routed[:, t, half, :], pick[:, :, :], AX.X, ALU.add))
                    V.need(f"expd{l}", t + 1)
                    V.step(v.tensor_reduce(ssum[:, t, :], ev, AX.X, ALU.add))
                    V.step(v.reciprocal(ssum[:, t, :], ssum[:, t, :]))
                    V.step(v.tensor_tensor(routed[:, t, 2, :].rearrange("p (h k) -> p h k", k=TOPK), ev,
                                           ssum[:, t, :].unsqueeze(2).broadcast_to([P, PEER_HEADS, TOPK]),
                                           ALU.mult), f"routed{l}")
                copied(dve, f"route{l}", TT - 1)
                base = ITEMS[f"hot{l}"][0]
                with dve.Fori(0, T // TOK_STEP) as i:
                    v.tensor_copy(route_now[:, :, :], route_t[:, :, bass.ds(i * TOK_STEP, TOK_STEP)])\
                        .then_inc(sem(f"route_now{l}"), 1)
                    dve.wait_ge(sem(f"route_now{l}"), i + 1)
                    for q in range(TOK_STEP // 4):
                        dve.wait_ge(bank_full, i * (TOK_STEP // 4) + base + q - 1)
                        for u in range(4):
                            s, tok = 4 * (q % 2) + u, 4 * q + u
                            v.tensor_scalar(hot_b(s), k1("iota"), route_now[:, 1, tok:tok + 1], None, ALU.is_equal)
                            v.tensor_scalar(hot_a(s), k1("iota"), route_now[:, 0, tok:tok + 1],
                                            route_now[:, 2, tok:tok + 1], ALU.is_equal, ALU.mult)\
                                .then_inc(sem(f"hot{l}"), 1)
                    dve.wait_ge(sem(f"hot{l}"), i * TOK_STEP + TOK_STEP)
                copied(dve, f"hot{l}", T // 4 - 1)
                base = ITEMS[f"down{l}"][0]
                with dve.Fori(0, KEYS // EXP_STEP) as i:
                    for e in range(EXP_STEP):
                        m = base + e
                        dve.wait_ge(bank_free[m % 4], i * (EXP_STEP // 4) + m // 4 + 1)
                        v.tensor_tensor(exp_w(e), exp_g(e),
                                        G[:, bass.ds(i * EXP_STEP + e, 1), :].rearrange("p a t -> p (a t)"),
                                        ALU.mult).then_inc(sem(f"weighted{l}"), 1)
                add_to_residual(f"up{l}")

            V.need("c2_loaded", 16)
            V.step(v.tensor_copy(x2[:, :, T:2 * T], x1[:, :, :]), "x_copied")
            for l in range(DEPTH):
                lo = 0 if l == 0 else T
                c = slice(lo, 2 * T)
                cols = [slice(s * T, (s + 1) * T) for s in range(2)]
                b = V.full(f"mod{l}")
                V.free(v.tensor_tensor(mod[:, :, :], b[:, 0:2 * N_MOD].rearrange("p (n s) -> p n s", s=2),
                                       k2("b_mod", l).unsqueeze(2).broadcast_to([P, N_MOD, 2]), ALU.add), f"mod{l}")
                for gs, g, chunk in ((gs1, "g1", 1), (gs2, "g2", 4)):
                    V.step(stt(gs[:, :, :], mod[:, chunk * KD:(chunk + 1) * KD, :], 1.0,
                               k2(g, l).unsqueeze(2).broadcast_to([P, KD, 2]), ALU.add, ALU.mult))

                def normalise_streams(item, gs, done, s0):
                    copied(dve, item, 0)
                    r = rnorm2[:, s0 * T:2 * T]
                    V.step(v.reciprocal(r, r))
                    for k in range(KD):
                        for s in range(s0, 2):
                            V.step(stt(h2[:, k, cols[s]], x2[:, k, cols[s]], gs[:, k, s:s + 1],
                                       rnorm2[:, cols[s]]), done, last=False)

                normalise_streams(f"norm2_{l}", gs1, f"hs2_{l}", 0)
                V.need("glu_zero", 1)
                for n in range(2):
                    copied(dve, f"fm{l}", 7 + n)
                    for s in range(lo // T, 2):
                        V.step(v.tensor_tensor(glu[:, n, s, CONV_PAD:CONV_PAD + T], ca[:, n, cols[s]],
                                               cv[:, n, cols[s]], ALU.mult))
                for j in range(3):
                    cj = slice(0 if j == 2 else lo, 2 * T)
                    copied(dve, f"hn2_{l}", j)
                    V.step(v.reciprocal(rs2[:, j, cj], rs2[:, j, cj]))
                    V.step(stt(raw2[:, j, cj], raw2[:, j, cj], k2("g_k" if j == 2 else "g_q", l), rs2[:, j, cj]),
                           f"qk_normed2_{l}")
                for j in range(2):
                    m = 2 - j
                    b = V.full(f"rot2_{l}", j)
                    q = raw2[:, 2 * j:2 * j + m, T:2 * T]
                    wide = lambda ap: ap[:, 0:m * T].rearrange("p (a b) -> p a b", b=T)
                    V.free(v.tensor_tensor(wide(rtmp2), wide(b), wide(k2("sin2")), ALU.mult), f"rot2_{l}", j)
                    V.step(v.tensor_tensor(q, q, wide(k2("cos2")), ALU.mult))
                    V.step(v.tensor_tensor(q, q, wide(rtmp2), ALU.add), f"rotated2_{l}")
                if l == 0:
                    attention(f"attc{l}", units2(False), prob2)
                attention(f"attx{l}", units2(True), prob2)
                for n in range(2):
                    w = k2("dw_w", l)[:, n * CONV:(n + 1) * CONV]
                    o = cv[:, n, c].rearrange("p (a b) -> p a b", b=T)
                    for j in range(CONV):
                        src = glu[:, n, lo // T:2, j:j + T]
                        if j == 0:
                            V.step(v.tensor_scalar(o, src, w[:, 0:1], k2("dw_b", l)[:, n:n + 1],
                                                   ALU.mult, ALU.add))
                        else:
                            V.step(stt(o, src, w[:, j:j + 1], o, ALU.mult, ALU.add),
                                   f"conv{l}" if j == CONV - 1 else None)
                b = V.full(f"mean{l}")
                V.step(v.tensor_tensor(cv[:, 0, c], cv[:, 0, c], b[:, c], ALU.subtract))
                V.free(v.tensor_tensor(cv[:, 1, c], cv[:, 1, c], b[:, c], ALU.subtract), f"mean{l}")
                copied(dve, f"var{l}", 0)
                V.step(v.reciprocal(rnorm2[:, c], rnorm2[:, c]))
                for n in range(2):
                    V.step(v.tensor_tensor(cv[:, n, c], cv[:, n, c], rnorm2[:, c], ALU.mult), f"conv_normed{l}")

                def add_gated(item, chunk):
                    for n in range(KD):
                        b = V.full(item, n)
                        for s in range(lo // T, 2):
                            o = x2[:, n, cols[s]]
                            ins = stt(o, b[:, cols[s]], mod[:, chunk * KD + n, s:s + 1], o, ALU.mult, ALU.add)
                            if s:
                                V.free(ins, item, n)

                add_gated(f"out2_{l}", 2)
                normalise_streams(f"fnorm2_{l}", gs2, f"hsf2_{l}", lo // T)
                for j in range(KF):
                    copied(dve, f"ffn{l}", 2 * j)
                    b = V.full(f"ffn{l}", 2 * j + 1)
                    V.free(v.tensor_tensor(hid[:, j, c], silu_a[:, j % 2, c], b[:, c], ALU.mult),
                           f"ffn{l}", 2 * j + 1)
                add_gated(f"ffo{l}", 5)


def tiles_of(w, order):
    k, n = w.shape
    t = w.reshape(k // P, P, n // P, P)
    t = t.transpose(2, 0, 1, 3) if order == "n" else t.transpose(0, 2, 1, 3)
    return t.reshape(-1, P, P)


def head_columns(start, order):
    return [start + h * HD + d for h in order for d in range(HD)]


def stream_parts(a):
    parts = []
    pad = []

    def put(w, order="n"):
        parts.append(tiles_of(w, order))

    def align():
        n = sum(p.shape[0] for p in parts)
        if n % BT:
            parts.append(np.zeros((-n % BT, P, P), np.float32))

    nw, qw, kw = NA_HEADS * HD, GQA_HEADS * HD, 2 * HD
    for l in range(DEPTH):
        w = a["w_in"][l]
        put(w[:, 0:2 * nw])
        put(w[:, head_columns(3 * nw, GQA_ORDER)])
        put(w[:, 3 * nw + qw:3 * nw + qw + kw])
        put(w[:, 2 * nw:3 * nw])
        put(w[:, 3 * nw + qw + kw:3 * nw + qw + 2 * kw])
        put(w[:, 3 * nw + qw + 2 * kw:])
        wa, wb = a["w_branch_na"][l], a["w_branch_swa"][l][head_columns(0, GQA_ORDER)]
        for j in range(4):
            put(wa[:, 2 * j * P:(2 * j + 2) * P])
            put(wb[:, 2 * j * P:(2 * j + 2) * P])
        put(a["w_out"][l])
        put(a["peer_query"][l])
        align()
        down = a["peer_down"][l].reshape(KEYS // 2, 2, KEYS, KD, P).transpose(0, 1, 3, 4, 2)
        up = a["peer_up"][l].reshape(KEYS // 2, 2, KEYS, KD, P).transpose(0, 1, 3, 2, 4)
        both = np.stack([down.reshape(KEYS // 2, 2 * KD, P, P), up.reshape(KEYS // 2, 2 * KD, P, P)], axis=1)
        parts.append(both.reshape(-1, P, P))
    for l in range(DEPTH):
        put(a["w_mod_2"][l])
        w = a["w_in_2"][l]
        put(w[:, head_columns(0, ATT2_ORDER)])
        put(w[:, 256:384])
        put(w[:, 512:768])
        put(w[:, 768:1280])
        put(w[:, 384:512])
        put(w[:, 1280:1536])
        put(a["w_fourier_2"][l])
        wp = a["w_pool_2"][l]
        bd = np.zeros((2, P, P), np.float32)
        for g in range(4):
            r = slice(HD * (g % 2), HD * (g % 2) + HD)
            bd[g // 2, r, r] = wp[g]
        parts.append(bd)
        put(a["w_conv_pw_2"][l])
        put(a["w_out_2"][l][head_columns(0, ATT2_ORDER) + list(range(256, D))])
        wf = a["w_ffn_in_2"][l]
        parts.append(np.stack([tiles_of(wf[:, :D_FF], "n").reshape(KF, KD, P, P),
                               tiles_of(wf[:, D_FF:], "n").reshape(KF, KD, P, P)], axis=1).reshape(-1, P, P))
        put(a["w_ffn_out_2"][l])
    return parts


def stream_array(a):
    parts = stream_parts(a)
    out = np.zeros((N_BLOCKS, P, BT, P), np.float32)
    at = 0
    for p in parts:
        done = 0
        while done < len(p):
            b, j = divmod(at, BT)
            if j == 0 and len(p) - done >= BT:
                m = (len(p) - done) // BT
                out[b:b + m] = p[done:done + m * BT].reshape(m, BT, P, P).transpose(0, 2, 1, 3)
                done, at = done + m * BT, at + m * BT
            else:
                m = min(BT - j, len(p) - done)
                out[b, :, j:j + m] = p[done:done + m].transpose(1, 0, 2)
                done, at = done + m, at + m
    return out.reshape(N_BLOCKS, P, BT * P)


def per_partition(v):
    return v.reshape(-1, P).T


def pack(table, width, values):
    out = np.zeros((P, width), np.float32)
    for name, (at, n) in table.items():
        out[:, at:at + n] = values[name]
    return out


def first_constants(a):
    v = {}
    v["ones_d"] = np.full((P, P), 1.0 / D)
    block = np.kron(np.eye(2), np.full((HD, HD), 1.0 / HD))
    v["head_mean"] = block
    half = HD // 2
    rot = np.zeros((HD, HD))
    rot[np.arange(half), np.arange(half) + half] = -1
    rot[np.arange(half) + half, np.arange(half)] = 1
    v["rot1"] = np.kron(np.eye(2), rot).T
    v["ident"] = np.eye(P)
    v["iota"] = np.tile(np.arange(P), (P, 1))
    v["iota16"] = np.tile(np.arange(TOPK), (P, 1))
    inv = (np.float32(THETA) ** (-np.arange(half, dtype=np.float32) / half)).astype(np.float32)
    ang = (np.arange(T, dtype=np.float32)[None, :] * inv[:, None]).astype(np.float32)
    v["cos1"] = np.tile(np.cos(ang), (4, 2))
    v["sin1"] = np.tile(np.sin(ang), (4, 2))
    q = np.arange(P)[:, None]
    k = np.arange(T)[None, :]
    v["swa_mask"] = np.concatenate(
        [np.where(np.abs(t * P + q - k) <= SWA_WINDOW, 0.0, MASKED) for t in range(TT)], axis=1)
    c = np.arange(GRID_W)
    cs = np.clip(c - WIN_COLS // 2, 0, GRID_W - WIN_COLS)
    inside = (c[None, :] >= cs[:, None]) & (c[None, :] < cs[:, None] + WIN_COLS)
    v["na_mask"] = np.tile(np.where(inside, 0.0, MASKED), (2, 2 * GRID_H))
    v["eps"] = np.full((P, 1), EPS)
    for l in range(DEPTH):
        v[f"g_mix{l}"] = per_partition(a["norm_mix"][l])
        v[f"g_ffn{l}"] = per_partition(a["norm_ffn"][l])
        v[f"g_qk{l}"] = np.tile(a["qk_norm"][l].T, (2, 1))
        v[f"gate_bias{l}"] = per_partition(a["gate_bias"][l].reshape(-1))
        v[f"sink{l}"] = np.tile(a["swa_sink"][l][GQA_ORDER], (P, 1))
        v[f"sub_keys{l}"] = a["peer_sub_keys"][l].transpose(2, 0, 1).reshape(P, 2 * KEYS)
    return pack(C1, C1_N, v)


def second_constants(a):
    v = {}
    v["ones_c"] = np.full((P, P), 1.0 / (2 * P))
    rot = np.zeros((HD, HD))
    ev = np.arange(0, HD, 2)
    rot[ev, ev + 1] = -1
    rot[ev + 1, ev] = 1
    v["rot2"] = np.kron(np.eye(2), rot).T
    n_freq = HD // 4
    inv = (np.float32(THETA) ** (-np.arange(n_freq, dtype=np.float32) / n_freq)).astype(np.float32)
    row = (np.arange(T) // GRID_W).astype(np.float32)
    col = (np.arange(T) % GRID_W).astype(np.float32)
    ang = np.concatenate([inv[:, None] * row, inv[:, None] * col], axis=0).astype(np.float32)
    ang = np.repeat(ang, 2, axis=0)
    v["cos2"] = np.tile(np.cos(ang), (2, 2))
    v["sin2"] = np.tile(np.sin(ang), (2, 2))
    turn = 2 * np.pi * np.outer(np.arange(HD), np.arange(HD)) / HD
    v["dft_d"] = np.concatenate([np.kron(np.eye(2), np.cos(turn)), np.kron(np.eye(2), np.sin(turn))], axis=1)
    turn = 2 * np.pi * (np.outer(np.arange(T), np.arange(T)) % T) / T
    norm = 1.0 / math.sqrt(T * HD)
    v["dft_n"] = np.concatenate(
        [m[t * P:(t + 1) * P] for t in range(TT) for m in (np.cos(turn) * norm, -np.sin(turn) * norm)], axis=1)
    pools = []
    s = np.arange(T)[:, None]
    t_ = np.arange(T)[None, :]
    for win in POOL_WINDOWS:
        lo = np.clip(t_ - win // 2, 0, T)
        hi = np.clip(t_ - win // 2 + win, 0, T)
        m = ((s >= lo) & (s < hi)) / (hi - lo) - np.eye(T)
        pools += [m[t * P:(t + 1) * P] for t in range(TT)]
    v["pool"] = np.concatenate(pools, axis=1)
    v["cond"] = np.stack([per_partition(a["c_ctx_2"]), per_partition(a["c_2"][0])], axis=2).reshape(P, 2 * KD)
    for l in range(DEPTH):
        v[f"b_mod{l}"] = per_partition(a["b_mod_2"][l])
        v[f"g1{l}"] = per_partition(a["g_norm1_2"][l])
        v[f"g2{l}"] = per_partition(a["g_norm2_2"][l])
        v[f"g_q{l}"] = np.tile(a["q_norm_g_2"][l], 2)[:, None]
        v[f"g_k{l}"] = np.tile(a["k_norm_g_2"][l], 2)[:, None]
        v[f"dw_w{l}"] = a["conv_dw_w_2"][l].T.reshape(2, P, CONV).transpose(1, 0, 2).reshape(P, 2 * CONV)
        v[f"dw_b{l}"] = per_partition(a["conv_dw_b_2"][l])
        v[f"ln_g{l}"] = per_partition(a["conv_ln_g_2"][l])
        v[f"ln_b{l}"] = per_partition(a["conv_ln_b_2"][l])
        v[f"pool_scale{l}"] = per_partition(a["pool_scale_2"][l])
    return pack(C2, C2_N, v)


def bias_array(rpb):
    tok = np.arange(T)
    r, c = tok // GRID_W, tok % GRID_W
    dr = r[None, :] - r[:, None] + WIN_ROWS - 1
    dc = np.clip(c[None, :] - c[:, None] + WIN_COLS - 1, 0, 2 * WIN_COLS - 2)
    full = rpb[:, :, dr, dc].reshape(DEPTH, NA_HEADS, TT, P, T)
    return full.transpose(0, 3, 1, 2, 4).reshape(DEPTH, P, NA_HEADS * TT * T)


def kernel(**inputs):
    import concourse.bacc as bacc
    from concourse.bass_utils import run_bass_kernel_spmd

    a = {name: np.asarray(value) for name, value in inputs.items()}
    arrays = {
        "stream": stream_array(a),
        "consts1": first_constants(a),
        "consts2": second_constants(a),
        "x_in": a["x"][0].T.reshape(KD, P, T),
        "ctx_in": a["ctx_2"][0].T.reshape(KD, P, T),
        "na_bias": bias_array(a["na_rpb"]),
    }
    arrays = {name: np.ascontiguousarray(value) for name, value in arrays.items()}
    nc = bacc.Bacc("TRN2", target_bir_lowering=False, num_devices=1)
    args = [nc.dram_tensor(name, value.shape, FP32, kind="ExternalInput").ap() for name, value in arrays.items()]
    out = nc.dram_tensor("out", (KD, P, T), FP32, kind="ExternalOutput").ap()
    program(nc, *args, out)
    r = run_bass_kernel_spmd(nc, [arrays], core_ids=[0])
    return np.ascontiguousarray(r.results[0]["out"].reshape(D, T).T.reshape(1, T, D))
```
